# Optimizing a Trainium2 kernel written in Bass

```python
import math
import jax, jax.numpy as jnp
from jax import lax
import numpy as np

D_MODEL = 2048
BATCH = 1
SEQ = 128
DEPTH = 1
DEC_BATCH = 1
DEC_SEQ = 256
PAST_LEN = 128

GRID_W = 64
D_MIX = D_MODEL
GLA_WIDTH = D_MIX // 2
GLA_HEADS = 4
GLA_DV = GLA_WIDTH // GLA_HEADS
GLA_DK = GLA_DV // 2
GLA_KDIM = GLA_HEADS * GLA_DK
GLA_RANK = 16
GLA_TAU = 16.0
GLA_CHUNK = 64
HY_WIDTH = D_MIX - GLA_WIDTH
HY_ORDER = 2
HY_SHORT = 3
HY_BANDS = 16
HY_PE_DIM = 1 + 2 * HY_BANDS
HY_FILTER_HIDDEN = 64
HY_TARGET = 1e-2
HY_FAST_PCT = 0.3
HY_SLOW_PCT = 1.5
N_GROUPS = 4
EXP_PER_GROUP = 4
N_EXPERTS = N_GROUPS * EXP_PER_GROUP
TOP_K_IN_GROUP = 2
D_EXPERT = D_MODEL // 4
N_IN_COLS = 2 * GLA_KDIM + 2 * GLA_WIDTH + 2 * GLA_RANK + (HY_ORDER + 1) * HY_WIDTH
EPS = 1e-6

kernel_name = 'hybrid_gla_hyena_hmoe_diffusion_step'

def _rmsnorm(x, g):
    xf = x.astype(jnp.float32)
    y = xf * lax.rsqrt(jnp.mean(xf * xf, axis=-1, keepdims=True) + EPS)
    return (y * g.astype(jnp.float32)).astype(x.dtype)

def _gla_chunked(q, k, v, log_a, s0):
    B, L, H, DK = q.shape
    DV = v.shape[-1]
    C = GLA_CHUNK
    NC = L // C
    q = q.reshape(B, NC, C, H, DK)
    k = k.reshape(B, NC, C, H, DK)
    v = v.reshape(B, NC, C, H, DV)
    b = jnp.cumsum(log_a.reshape(B, NC, C, H, DK), axis=2)
    b_last = b[:, :, -1]
    q_t = q * jnp.exp(b)
    k_t = k * jnp.exp(-b)
    mask = jnp.tril(jnp.ones((C, C), dtype=bool))
    att = jnp.einsum('bnihk,bnjhk->bnhij', q_t, k_t)
    att = jnp.where(mask, att, 0.0)
    o_intra = jnp.einsum('bnhij,bnjhv->bnihv', att, v)
    k_s = k * jnp.exp(b_last[:, :, None] - b)
    upd = jnp.einsum('bnjhk,bnjhv->bnhkv', k_s, v)
    decay = jnp.exp(b_last)

    def step(S, inp):
        d, u = inp
        return d[..., None] * S + u, S

    s_final, s_in = lax.scan(step, s0, (jnp.moveaxis(decay, 1, 0), jnp.moveaxis(upd, 1, 0)))
    s_in = jnp.moveaxis(s_in, 0, 1)
    o_inter = jnp.einsum('bnihk,bnhkv->bnihv', q_t, s_in)
    return (o_intra + o_inter).reshape(B, L, H, DV), s_final

def _short_conv(u, w, b, n_seg):
    B, L, C = u.shape
    seg = L // n_seg
    pad = HY_SHORT // 2
    us = jnp.pad(u.reshape(B, n_seg, seg, C), ((0, 0), (0, 0), (pad, pad), (0, 0)))
    y = sum(us[:, :, j:j + seg] * w[j] for j in range(HY_SHORT)) + b
    return y.reshape(B, L, C)

def _hyena_filters(L, w1, b1, w2, b2, w3, freq):
    f32 = jnp.float32
    t = jnp.arange(L, dtype=f32)
    t01 = t / max(L - 1, 1)
    ang = 2.0 * math.pi * t / L
    bands = jnp.linspace(1e-4, HY_BANDS - 1, HY_BANDS, dtype=f32)
    pe = jnp.concatenate([t01[:, None], jnp.cos(ang[:, None] * bands), -jnp.sin(ang[:, None] * bands)], axis=-1)
    fr = freq.astype(f32)
    hdn = jnp.sin(fr * (pe @ w1.astype(f32) + b1.astype(f32)))
    hdn = jnp.sin(fr * (hdn @ w2.astype(f32) + b2.astype(f32)))
    filt = (hdn @ w3.astype(f32)).reshape(L, 2, HY_ORDER, HY_WIDTH)
    deltas = jnp.abs(jnp.linspace(math.log(HY_TARGET) / HY_SLOW_PCT, math.log(HY_TARGET) / HY_FAST_PCT, HY_WIDTH, dtype=f32))
    filt = filt * jnp.exp(-t01[:, None] * deltas)[:, None, None, :]
    filt = filt / jnp.sum(jnp.abs(filt), axis=(0, 1), keepdims=True)
    full = jnp.concatenate([filt[:, 0], jnp.zeros((1, HY_ORDER, HY_WIDTH), f32), jnp.flip(filt[1:, 1], axis=0)], axis=0)
    return jnp.fft.rfft(full, axis=0)

def _mixer(h, s0_f, s0_b, n_seg, l, p):
    B, L, _ = h.shape
    f32 = jnp.float32
    proj = h @ p['w_in'][l]
    sizes = (GLA_KDIM, GLA_KDIM, GLA_WIDTH, GLA_WIDTH, GLA_RANK, GLA_RANK, (HY_ORDER + 1) * HY_WIDTH)
    q, k, v, g, lr_f, lr_b, u_hy = jnp.split(proj, np.cumsum(sizes)[:-1].tolist(), axis=-1)
    q = q.astype(f32).reshape(B, L, GLA_HEADS, GLA_DK) * (GLA_DK ** -0.5)
    k = k.astype(f32).reshape(B, L, GLA_HEADS, GLA_DK)
    v = v.astype(f32).reshape(B, L, GLA_HEADS, GLA_DV)
    la_f = jax.nn.log_sigmoid((lr_f @ p['w_dec_f'][l] + p['b_dec_f'][l]).astype(f32)).reshape(B, L, GLA_HEADS, GLA_DK) / GLA_TAU
    la_b = jax.nn.log_sigmoid((lr_b @ p['w_dec_b'][l] + p['b_dec_b'][l]).astype(f32)).reshape(B, L, GLA_HEADS, GLA_DK) / GLA_TAU
    o_f, s_f = _gla_chunked(q, k, v, la_f, s0_f.astype(f32))
    o_b, s_b = _gla_chunked(jnp.flip(q, 1), jnp.flip(k, 1), jnp.flip(v, 1), jnp.flip(la_b, 1), s0_b.astype(f32))
    o = _rmsnorm(o_f + jnp.flip(o_b, 1), p['g_gla'][l]).reshape(B, L, GLA_WIDTH)
    y_gla = (o * jax.nn.silu(g.astype(f32))).astype(h.dtype)
    u_hy = _short_conv(u_hy, p['hy_conv_w'][l], p['hy_conv_b'][l], n_seg)
    parts = jnp.split(u_hy.astype(f32), HY_ORDER + 1, axis=-1)
    filt_f = _hyena_filters(L, p['hy_w1'][l], p['hy_b1'][l], p['hy_w2'][l], p['hy_b2'][l], p['hy_w3'][l], p['hy_freq'][l])
    z = parts[0]
    for n in range(HY_ORDER):
        conv = jnp.fft.irfft(jnp.fft.rfft(z, n=2 * L, axis=1) * filt_f[None, :, n], n=2 * L, axis=1)[:, :L]
        z = parts[n + 1] * (conv + p['hy_bias'][l, n].astype(f32) * z)
    y_hy = _rmsnorm(z, p['g_hy'][l]).astype(h.dtype)
    y = jnp.concatenate([y_gla, y_hy], axis=-1) @ p['w_out'][l]
    return y, s_f, s_b

def _moe(h, l, p):
    B, L, D = h.shape
    f32 = jnp.float32
    t = h.reshape(B * L, D)
    lg = (t @ p['w_router_grp'][l] + p['b_router_grp'][l]).astype(f32)
    pg = jax.nn.softmax(lg, axis=-1)
    grp = jnp.argmax(lg, axis=-1)
    p_grp = jnp.take_along_axis(pg, grp[:, None], axis=1)[:, 0]
    le = (t @ p['w_router_exp'][l] + p['b_router_exp'][l]).astype(f32).reshape(-1, N_GROUPS, EXP_PER_GROUP)
    le_sel = jnp.take_along_axis(le, grp[:, None, None], axis=1)[:, 0]
    top_v, top_i = lax.top_k(jax.nn.softmax(le_sel, axis=-1), TOP_K_IN_GROUP)
    top_v = top_v / jnp.sum(top_v, axis=-1, keepdims=True)
    ids = grp[:, None] * EXP_PER_GROUP + top_i
    gates = jnp.sum(jax.nn.one_hot(ids, N_EXPERTS, dtype=f32) * (p_grp[:, None] * top_v)[..., None], axis=1)
    out = jnp.zeros((B * L, D), f32)
    for e in range(N_EXPERTS):
        he = jax.nn.silu(t @ p['w_exp_gate'][l, e]) * (t @ p['w_exp_up'][l, e])
        out = out + gates[:, e:e + 1] * (he @ p['w_exp_down'][l, e]).astype(f32)
    return out.reshape(B, L, D).astype(h.dtype)

def _layer(x, cond, s0_f, s0_b, n_seg, l, p):
    mod = jax.nn.silu(cond) @ p['w_ada'][l] + p['b_ada'][l]
    sh1, sc1, gt1, sh2, sc2, gt2 = jnp.split(mod[:, None, :], 6, axis=-1)
    h = _rmsnorm(x, p['g_pre_mix'][l]) * (1.0 + sc1) + sh1
    y, s_f, s_b = _mixer(h, s0_f, s0_b, n_seg, l, p)
    x = x + gt1 * _rmsnorm(y, p['g_post_mix'][l])
    h = _rmsnorm(x, p['g_pre_ffn'][l]) * (1.0 + sc2) + sh2
    y = _moe(h, l, p)
    x = x + gt2 * _rmsnorm(y, p['g_post_ffn'][l])
    return x, s_f, s_b

def setup_inputs(seed: int = 0) -> dict:
    key = jax.random.key(seed)
    ks = iter(jax.random.split(key, 48))

    def nrm(shape, scale):
        return jax.random.normal(next(ks), shape, jnp.float32) * scale

    def gain(shape):
        return 1.0 + nrm(shape, 0.05)

    D = D_MODEL
    return {
        'x_prompt': nrm((BATCH, SEQ, D), 1.0),
        'x_sample': nrm((DEC_BATCH, DEC_SEQ, D), 1.0),
        'c': nrm((DEC_BATCH, D), 1.0),
        'state_gla_fwd': nrm((DEC_BATCH, DEPTH, GLA_HEADS, GLA_DK, GLA_DV), 1.0),
        'state_gla_bwd': nrm((DEC_BATCH, DEPTH, GLA_HEADS, GLA_DK, GLA_DV), 1.0),
        'c_ctx': nrm((D,), 1.0),
        'w_ada': nrm((DEPTH, D, 6 * D), 0.5 * D ** -0.5),
        'b_ada': nrm((DEPTH, 6 * D), 0.02),
        'g_pre_mix': gain((DEPTH, D)),
        'g_post_mix': gain((DEPTH, D)),
        'g_pre_ffn': gain((DEPTH, D)),
        'g_post_ffn': gain((DEPTH, D)),
        'w_in': nrm((DEPTH, D, N_IN_COLS), D ** -0.5),
        'w_dec_f': nrm((DEPTH, GLA_RANK, GLA_KDIM), GLA_RANK ** -0.5),
        'b_dec_f': nrm((DEPTH, GLA_KDIM), 0.1),
        'w_dec_b': nrm((DEPTH, GLA_RANK, GLA_KDIM), GLA_RANK ** -0.5),
        'b_dec_b': nrm((DEPTH, GLA_KDIM), 0.1),
        'g_gla': gain((DEPTH, GLA_DV)),
        'hy_conv_w': nrm((DEPTH, HY_SHORT, (HY_ORDER + 1) * HY_WIDTH), HY_SHORT ** -0.5),
        'hy_conv_b': nrm((DEPTH, (HY_ORDER + 1) * HY_WIDTH), 0.02),
        'hy_w1': nrm((DEPTH, HY_PE_DIM, HY_FILTER_HIDDEN), HY_PE_DIM ** -0.5),
        'hy_b1': nrm((DEPTH, HY_FILTER_HIDDEN), 0.1),
        'hy_w2': nrm((DEPTH, HY_FILTER_HIDDEN, HY_FILTER_HIDDEN), HY_FILTER_HIDDEN ** -0.5),
        'hy_b2': nrm((DEPTH, HY_FILTER_HIDDEN), 0.1),
        'hy_w3': nrm((DEPTH, HY_FILTER_HIDDEN, 2 * HY_ORDER * HY_WIDTH), HY_FILTER_HIDDEN ** -0.5),
        'hy_freq': gain((DEPTH, HY_FILTER_HIDDEN)),
        'hy_bias': nrm((DEPTH, HY_ORDER, HY_WIDTH), 0.1),
        'g_hy': gain((DEPTH, HY_WIDTH)),
        'w_out': nrm((DEPTH, D_MIX, D), D_MIX ** -0.5),
        'w_router_grp': nrm((DEPTH, D, N_GROUPS), D ** -0.5),
        'b_router_grp': nrm((DEPTH, N_GROUPS), 0.01),
        'w_router_exp': nrm((DEPTH, D, N_EXPERTS), D ** -0.5),
        'b_router_exp': nrm((DEPTH, N_EXPERTS), 0.01),
        'w_exp_gate': nrm((DEPTH, N_EXPERTS, D, D_EXPERT), D ** -0.5),
        'w_exp_up': nrm((DEPTH, N_EXPERTS, D, D_EXPERT), D ** -0.5),
        'w_exp_down': nrm((DEPTH, N_EXPERTS, D_EXPERT, D), D_EXPERT ** -0.5),
    }

def reference(x_prompt, x_sample, c, state_gla_fwd, state_gla_bwd, c_ctx, w_ada, b_ada,
              g_pre_mix, g_post_mix, g_pre_ffn, g_post_ffn, w_in, w_dec_f, b_dec_f, w_dec_b, b_dec_b,
              g_gla, hy_conv_w, hy_conv_b, hy_w1, hy_b1, hy_w2, hy_b2, hy_w3, hy_freq, hy_bias, g_hy,
              w_out, w_router_grp, b_router_grp, w_router_exp, b_router_exp, w_exp_gate, w_exp_up, w_exp_down):
    p = dict(w_ada=w_ada, b_ada=b_ada, g_pre_mix=g_pre_mix, g_post_mix=g_post_mix, g_pre_ffn=g_pre_ffn,
             g_post_ffn=g_post_ffn, w_in=w_in, w_dec_f=w_dec_f, b_dec_f=b_dec_f, w_dec_b=w_dec_b, b_dec_b=b_dec_b,
             g_gla=g_gla, hy_conv_w=hy_conv_w, hy_conv_b=hy_conv_b, hy_w1=hy_w1, hy_b1=hy_b1, hy_w2=hy_w2,
             hy_b2=hy_b2, hy_w3=hy_w3, hy_freq=hy_freq, hy_bias=hy_bias, g_hy=g_hy, w_out=w_out,
             w_router_grp=w_router_grp, b_router_grp=b_router_grp, w_router_exp=w_router_exp,
             b_router_exp=b_router_exp, w_exp_gate=w_exp_gate, w_exp_up=w_exp_up, w_exp_down=w_exp_down)
    rows = x_sample.shape[1] // GRID_W
    zero_state = jnp.zeros((x_prompt.shape[0], GLA_HEADS, GLA_DK, GLA_DV), jnp.float32)
    y_p = x_prompt
    y_s = x_sample
    new_f = []
    new_b = []
    for l in range(DEPTH):
        y_p, s_f, s_b = _layer(y_p, c_ctx[None, :], zero_state, zero_state, 1, l, p)
        new_f.append(s_f.astype(x_prompt.dtype))
        new_b.append(s_b.astype(x_prompt.dtype))
        y_s, _, _ = _layer(y_s, c, state_gla_fwd[:, l], state_gla_bwd[:, l], rows, l, p)
    new_state_gla_fwd = jnp.stack(new_f, axis=1)
    new_state_gla_bwd = jnp.stack(new_b, axis=1)
    return (y_p, y_s, new_state_gla_fwd, new_state_gla_bwd)


_drawn_inputs = setup_inputs


def setup_inputs(seed=0):
    import zlib

    import numpy as np

    out = dict(_drawn_inputs(seed))
    spreads = {}
    factors = {'state_gla_fwd': 8.0, 'g_post_ffn': 4.256}
    for name, (base, spread) in spreads.items():
        noise = np.random.default_rng([zlib.crc32(name.encode()), seed]).standard_normal(out[name].shape)
        drawn = base * np.exp(spread * noise) if base else spread * noise
        out[name] = __import__('jax').numpy.asarray(drawn.astype(out[name].dtype))
    for name, factor in factors.items():
        out[name] = (out[name] * factor).astype(out[name].dtype)
    return out
```

```python
import math
from contextlib import ExitStack

import numpy as np

import concourse.bass as bass
from concourse import mybir

F32 = mybir.dt.float32
I32 = mybir.dt.int32
ALU = mybir.AluOpType
ACT = mybir.ActivationFunctionType
AX = mybir.AxisListType

P = 128
D = 2048
KT = D // P
SEQ, DEC = 128, 256
NT = (SEQ + DEC) // P
TOK = NT * P
COND = [0, 1, 1]
HEADS, DK, DV, CHUNK = 4, 128, 256, 64
NCH = TOK // CHUNK
RANK = 16
TAU = 16.0
HYW = 1024
HALF = HYW // 2
BANDS, HID = 16, 64
PE_DIM = 1 + 2 * BANDS
NG, EPG = 4, 4
NE = NG * EPG
DE = 512
EPS = 1e-6
NCOL = 512
COL_Q, COL_K, COL_V, COL_G = 0, 512, 1024, 2048
COL_LR, COL_HY = 3072, 3104
SLOT = 4096
RING = 3
BLK = 64
MAXB = NE + (2 * TOK - 2) // BLK
MAGIC = 1.5 * 2.0 ** 23
TWO_PI_HI = 6.28125
TWO_PI_LO = 2 * math.pi - TWO_PI_HI
PI_SAFE = 3.1415925

SEQS = [dict(tiles=[0], re=[0], im=[1]), dict(tiles=[1, 2], re=[2, 3], im=[4, 5])]
NROW = 6
FWD, INV = {}, {}
for _s in SEQS:
    for _t in _s["tiles"]:
        for _r in _s["re"] + _s["im"]:
            FWD[_t, _r] = len(FWD)
for _s in SEQS:
    for _r in _s["re"] + _s["im"]:
        for _t in _s["tiles"]:
            INV[_r, _t] = len(FWD) + len(INV)


def shape_constants():
    ident = np.eye(P, dtype=np.float32)
    tri = np.triu(np.ones((P, P), np.float32), 1)
    sel = np.zeros((P, 2, P), np.float32)
    for j in range(4):
        for c in range(2):
            sel[32 * j + c, c] = 1
    base = np.concatenate([ident, tri, sel.reshape(P, 2 * P)], 1)
    masks = np.zeros((P, 2, P), np.int32)
    i = np.arange(P)
    same = (i[:, None] // CHUNK) == (i[None, :] // CHUNK)
    masks[:, 0] = same & (i[:, None] <= i[None, :])
    masks[:, 1] = same & (i[:, None] >= i[None, :])
    dft = np.zeros((P, len(FWD) + len(INV), P), np.float64)
    for s in SEQS:
        n = P * len(s["tiles"])
        for a, t in enumerate(s["tiles"]):
            taps = a * P + i
            for part, fn in (("re", np.cos), ("im", np.sin)):
                for b, r in enumerate(s[part]):
                    w = (b * P + i + 0.5) * np.pi / n
                    dft[:, FWD[t, r]] = fn(taps[:, None] * w[None, :])
                    dft[:, INV[r, t]] = fn(w[:, None] * taps[None, :]) / n
    pe, decay = np.zeros((PE_DIM, TOK), np.float32), np.zeros((P, NT, HYW), np.float32)
    bands = np.linspace(1e-4, BANDS - 1, BANDS, dtype=np.float32).astype(np.float64)
    rate = np.abs(np.linspace(math.log(1e-2) / 1.5, math.log(1e-2) / 0.3, HYW, dtype=np.float32))
    for s in SEQS:
        n = P * len(s["tiles"])
        for a, t in enumerate(s["tiles"]):
            taps = (a * P + i).astype(np.float64)
            ang = (2 * np.pi * taps / n)[:, None] * bands
            t01 = taps / (n - 1)
            pe[:, t * P:(t + 1) * P] = np.concatenate([t01[:, None], np.cos(ang), -np.sin(ang)], 1).T
            decay[:, t] = np.exp(-t01[:, None] * rate.astype(np.float64))
    return dict(k_base=base, k_masks=masks, k_dft=dft.astype(np.float32).reshape(P, -1), k_pe=pe, k_decay=decay)


class Engine:

    def __init__(self, eng, step_sem):
        self.e, self.step, self.n, self.last = eng, step_sem, {}, None

    def op(self, ins, sem=None):
        sem = self.step if sem is None else sem
        ins.then_inc(sem, 1)
        self.n[sem.name] = self.n.get(sem.name, 0) + 1
        self.last = (sem, self.n[sem.name])

    def sync(self):
        self.e.wait_ge(*self.last)


ARENA = 26112
MIX = 6144


def build(nc, T):
    ctx = ExitStack()
    with ctx:
        def sb(name, shape, dt=F32):
            return ctx.enter_context(nc.sbuf_tensor("s_" + name, shape, dt))

        sems = {}

        def S(name):
            if name not in sems:
                sems[name] = ctx.enter_context(nc.semaphore(name))
            return sems[name]

        ring_mem = sb("ring", [P, RING * SLOT])
        arena = sb("arena", [P, ARENA])
        hT = sb("hT", [P, KT, TOK])
        mod = sb("mod", [P, 6, NCOL])
        gain = sb("gain", [P, 4, NCOL])
        base = sb("base", [P, 4 * P])
        masks = sb("masks", [P, 2, P], I32)
        ones = sb("ones", [P, P])
        reset = sb("reset", [P, TOK])
        attm = sb("attm", [P, 2, 2, P])
        sT = sb("sT", [P, KT, 32])
        colA = sb("colA", [P, 50])
        colB = sb("colB", [P, 96])
        hdn = sb("hdn", [HID, TOK])
        stat = sb("stat", [P, 64])
        decs = sb("decs", [P, 2, HEADS, NCH])
        slot_i = sb("slot_i", [P, 2, NT], I32)
        wpair = sb("wpair", [P, 2, NT])
        tok_i = sb("tok_i", [P, NT], I32)
        tab_i = sb("tab_i", [P, MAXB + 2 + NE], I32)
        idx_i = sb("idx_i", [BLK, 1], I32)
        ident, tri = base[:, 0:P], base[:, P:2 * P]
        sel = base[:, 2 * P:4 * P].rearrange("p (c m) -> p c m", c=2)
        ps = ctx.enter_context(nc.psum_tensor("ps", [P, 8, NCOL], F32))

        def region(start, *shape, rows=P):
            n = int(np.prod(shape))
            assert start + n <= ARENA, (start, n)
            v = arena[0:rows, start:start + n]
            if len(shape) == 1:
                return v
            names = "abcde"[:len(shape)]
            sizes = dict(zip(names, shape))
            return v.rearrange(f"p ({' '.join(names)}) -> p {' '.join(names)}", **sizes)

        x_sb = region(2 * MIX, NT, D)
        y_sb = region(3 * MIX, NT, D)
        h_tm = region(0, NT, D)
        w1s = region(24576, HID, rows=PE_DIM)
        w2s = region(24640, HID, rows=HID)
        pe_sb = region(24704, TOK, rows=PE_DIM)
        ftmp = region(25088, 2, TOK, rows=HID)
        rowsA = region(25856, P, rows=50)
        rowsB = region(25984, P, rows=96)
        wlr = region(21504, KT, 2 * RANK)
        wdec = region(22016, 2, NCOL, rows=2 * RANK)
        lrT = region(23040, TOK, rows=2 * RANK)
        fcol = region(23424, 4, rows=HID)
        zero_i = region(23428, P, rows=(MAXB + 1) * BLK // P).bitcast(I32)
        qf = region(0, HEADS, TOK)
        kf = region(1536, HEADS, TOK)
        Tb = [region(3072 + 1536 * d, HEADS, TOK) for d in range(2)]
        Pb = [region(MIX + 3072 * d, HEADS, TOK) for d in range(2)]
        Bb = [region(MIX + 1536 + 3072 * d, HEADS, TOK) for d in range(2)]
        ksT = [region(2 * MIX + 1536 * d, NT, HEADS * DK) for d in range(2)]
        vtm = region(2 * MIX + 3072, NT, HEADS * DV)
        gtm = region(3 * MIX, NT, HEADS * DV)
        Sst = region(21504, 2, 6, DV)
        zx = region(0, 3, NT, HALF)
        hyT = region(4608, 4, TOK)
        Gs = region(MIX, NROW, HALF)
        ff = region(MIX + 3072, NT, 2, HALF)
        fs = region(MIX + 6144, NT, HALF)
        Yb = region(MIX + 3072, NROW, HALF)
        tA = region(MIX + 6144, HALF)
        tB = region(MIX + 6144 + 512, HALF)
        dft = region(MIX + 7680, 20, P)
        decay = region(16384, NT, HALF)
        z2 = region(21504, NT, 2, HALF)
        w3 = region(24576, 2, HALF, rows=HID)
        biasr = region(25600, HALF)
        wr = region(24576, KT, NG + NE)
        br = region(24576 + 320, NG + NE)
        rt_at = [21504]

        def small(*shape):
            v = region(rt_at[0], *shape)
            rt_at[0] += int(np.prod(shape))
            return v

        r_log, r_ex, r_grp = small(NT, NG + NE), small(2, NT, 4), small(NT, 4)
        r_t4, r_pri, r_oh = small(NT, 4), small(NT, 4), small(2, NT, 4)
        r_top, r_t1, r_pg, r_m2 = small(NT), small(NT), small(NT), small(NT)
        r_one, r_pair, r_slot = small(2, NT, NE), small(NT, NE), small(NT, NE)
        r_nb, r_end, r_first, r_tab = small(NE), small(NE), small(NE), small(MAXB + 2 + NE)
        r_cmp = small(MAXB, NE)
        junk = region(25600, DV)
        mring = [ring_mem[:, SLOT * s:SLOT * (s + 1)] if s < RING else arena[:, SLOT * (s - RING):SLOT * (s - RING + 1)]
                 for s in range(6)]
        hg = region(18432, D, rows=BLK)
        ysl = region(18432 + D, 2, NCOL)
        hflat = hT[:, :, :].rearrange("p k t -> p (k t)")
        hgT = hflat[:, 0:KT * BLK].rearrange("p (k s) -> p k s", k=KT)
        heT = hflat[:, 2048:2048 + 4 * BLK].rearrange("p (k s) -> p k s", k=4)
        he = hflat[0:BLK, 2560:3072]
        sg = hflat[0:BLK, 3072:3584]
        yga = [[region((2 * t + r) * D, D) for r in range(2)] for t in range(NT)]
        gate_b = region(21504, 2, D)

        h_dram = nc.dram_tensor("h_rows", [TOK, D], F32).ap()
        y_dram = nc.dram_tensor("y_slots", [(MAXB + 1) * BLK, D], F32).ap()
        tok_dram = nc.dram_tensor("tok_of_slot", [(MAXB + 1) * BLK, 1], I32).ap()

        x_rows = [T["x_prompt"][0], T["x_sample"][0, 0:P], T["x_sample"][0, P:2 * P]]
        out_rows = [T["y_prompt"][0], T["y_sample"][0, 0:P], T["y_sample"][0, P:2 * P]]

        uses, used = {}, {b: [] for b in range(8)}

        def nth_read(reader, key):
            names = used[uses[key][0]]
            return sum(reader in uses[k][1] for k in names[:uses[key][2]])

        def wait_read(eng, reader, key):
            eng.wait_ge(S(f"free_{reader}{uses[key][0]}"), nth_read(reader, key))

        def take(pe, bank, key, readers=("dve",)):
            assert key not in uses, key
            if used[bank]:
                for r in uses[used[bank][-1]][1]:
                    wait_read(pe, r, used[bank][-1])
            uses[key] = (bank, readers, len(used[bank]) + 1)
            used[bank].append(key)

        def filled(key):
            return S(f"full{uses[key][0]}")

        def read(eng, key):
            bank, _, nth = uses[key]
            eng.wait_ge(S(f"full{bank}"), nth)
            return bank

        def freed(reader, key):
            return S(f"free_{reader}{uses[key][0]}")

        loads, released = [], []

        def slot_view(i):
            return ring_mem[:, SLOT * (i % RING):SLOT * (i % RING + 1)]

        def next_slot(pe, src):
            i = len(loads)
            loads.append(src)
            pe.wait_ge(S(f"ring{i % RING}"), 16 * (i // RING + 1))
            return slot_view(i).rearrange("p (k n) -> p k n", k=8)

        def slot_done(ins, key=None):
            if key is None:
                n = 1 + sum(s is S("ring_used") for s, _ in released)
                ins.then_inc(S("ring_used"), 1)
                released.append((S("ring_used"), n))
            else:
                ins.then_inc(filled(key), 1)
                released.append((filled(key), uses[key][2]))

        def w_block(w, row0, col0):
            return w[row0:row0 + 8 * P, col0:col0 + NCOL].rearrange("(k p) n -> p k n", p=P)

        w_ada, w_in, w_out = T["w_ada"][0], T["w_in"][0], T["w_out"][0]

        SCAN = [[(0, None, 0), (1, 0, 1), (2, 2, 3), (3, 3, 4), (4, 4, 5)],
                [(1, None, 0), (0, 0, 1), (5, 2, 3), (4, 3, 4), (3, 4, 5)]]
        STATE_IN = [{1: 0, 2: 2, 3: 3, 4: 4, 5: 5}, {0: 0, 5: 2, 4: 3, 3: 4, 2: 5}]
        ADA_BANK = 6
        ADA_KEYS = ["ada0", "ada1", "ada2", "ada3", "ada4", "ada5"]
        HYENA_BLOCKS = [(0, 0, None), (0, 1, None), (0, 2, 0), (1, 1, 1), (1, 0, 2), (1, 2, 3)]
        HYENA_ADA = [(1, 2), (1, 2), (0, 1), (0, 1), (0, 1), (0, 0)]
        TURNED = {c: f"zx{hb}{part}{NT - 1}" for hb, part, c in HYENA_BLOCKS if c is not None}

        block = ctx.enter_context(nc.Block())

        @block.tensor
        def _(pe):
            mm, tr = nc.tensor.matmul, nc.tensor.transpose

            pe.wait_ge(S("in_base"), 16)
            pe.wait_ge(S("in_rowsA"), 16 * 6)
            take(pe, 5, "colA")
            tr(ps[:, 5, 0:50], rowsA, ident[0:50, 0:50]).then_inc(filled("colA"), 1)
            pe.wait_ge(S("in_rowsB"), 32)
            take(pe, 4, "colB")
            tr(ps[:, 4, 0:96], rowsB, ident[0:96, 0:96]).then_inc(filled("colB"), 1)
            pe.wait_ge(S("in_mlp"), 16 * 6)
            take(pe, 3, "hid1")
            mm(ps[0:HID, 3, 0:TOK], w1s, pe_sb, start=True, stop=True).then_inc(filled("hid1"), 1)

            ada_at = [0]

            def ada_step():
                third, k = divmod(ada_at[0], KT)
                ada_at[0] += 1
                w = next_slot(pe, w_ada[k * P:(k + 1) * P, third * SLOT:(third + 1) * SLOT])
                for n in range(8):
                    bank, j = ADA_BANK + n // 4, n % 4
                    key = ADA_KEYS[third * 2 + n // 4]
                    if k == 0 and j == 0:
                        take(pe, bank, key)
                    m = mm(ps[32 * j:32 * j + 32, bank, :], sT[:, k, :], w[:, n, :], start=(k == 0),
                           stop=(k == KT - 1), skip_group_check=True)
                    if k == KT - 1 and n == 3:
                        m.then_inc(filled(key), 1)
                slot_done(m, key if k == KT - 1 else None)

            pe.wait_ge(S("sT_ready"), 2)
            for _ in range(KT):
                ada_step()
            pe.wait_ge(S("hid_ready"), 1)
            take(pe, 3, "hid2")
            mm(ps[0:HID, 3, 0:TOK], w2s, ftmp[:, 1, :], start=True, stop=True).then_inc(filled("hid2"), 1)

            def modulate(ph):
                def rows(j):
                    for q, w, b0 in ((3 * ph + 1, "scale", (4, 6)[j % 2]), (3 * ph, "shift", 2)):
                        for c in range(2):
                            key = f"{w}{ph}{j}{c}"
                            take(pe, b0 + c, key)
                            mm(ps[:, b0 + c, :], sel[32 * j:32 * j + 2, c, :], mod[32 * j:32 * j + 2, q, :],
                               start=True, stop=True).then_inc(filled(key), 1)

                rows(0)
                for j in range(4):
                    if j < 3:
                        rows(j + 1)
                    wait_read(pe, "dve", f"shift{ph}{j}1")
                    for kt in range(4 * j, 4 * j + 4):
                        take(pe, kt % 2, f"hT{ph}_{kt}", ("act",))
                        for t in range(NT):
                            m = tr(ps[:, kt % 2, t * P:(t + 1) * P], h_tm[:, t, kt * P:(kt + 1) * P], ident)
                        m.then_inc(filled(f"hT{ph}_{kt}"), 1)

            pe.wait_ge(S("mod_ready"), 1)
            modulate(0)

            def project(key, kind, w, col0, readers=("act",), ada=(0, 0), between=None,
                        banks=(0, 1, 2, 3)):
                n = 4 if kind == "fm" else NT
                for kh in range(2):
                    v = next_slot(pe, w_block(w, kh * 8 * P, col0))
                    for m_ in range(n):
                        bk = f"{key}_{m_}"
                        if kh == 0:
                            take(pe, banks[m_], bk, readers)
                        for k in range(8):
                            kk = kh * 8 + k
                            if kind == "fm":
                                m = mm(ps[:, banks[m_], 0:TOK], v[:, k, m_ * P:(m_ + 1) * P], hT[:, kk, :],
                                       start=(kk == 0), stop=(kk == KT - 1))
                            else:
                                m = mm(ps[:, banks[m_], :], hT[:, kk, m_ * P:(m_ + 1) * P], v[:, k, :],
                                       start=(kk == 0), stop=(kk == KT - 1))
                        if kh == 1 and m_ < n - 1:
                            m.then_inc(filled(bk), 1)
                    slot_done(m, bk if kh == 1 else None)
                    for _ in range(ada[kh]):
                        ada_step()
                    if kh == 0 and between:
                        between()

            wait_read(pe, "act", f"hT0_{KT - 1}")
            pe.wait_ge(S("in_lr"), 16)
            take(pe, 4, "lr", ("act",))
            for k in range(KT):
                m = mm(ps[0:2 * RANK, 4, 0:TOK], wlr[:, k, :], hT[:, k, :], start=(k == 0), stop=(k == KT - 1))
            m.then_inc(filled("lr"), 1)
            project("q", "fm", w_in, COL_Q, ada=(1, 2))
            wait_read(pe, "act", "lr")
            pe.wait_ge(S("in_dec"), 32)
            for d in range(2):
                for h in range(HEADS):
                    take(pe, 4 + h % 2, f"la{d}{h}", ("act", "dve"))
                    mm(ps[:, 4 + h % 2, 0:TOK], wdec[:, d, h * DK:(h + 1) * DK], lrT,
                       start=True, stop=True).then_inc(filled(f"la{d}{h}"), 1)
            project("k", "fm", w_in, COL_K, ada=(1, 2))
            project("v0", "tm", w_in, COL_V, ada=(1, 2))
            project("v1", "tm", w_in, COL_V + NCOL, ada=(1, 2))
            for d in range(2):
                pe.wait_ge(S("ks_ready"), d + 1)
                for t in range(NT):
                    take(pe, 4 + t % 2, f"ks{d}{t}", ("act",))
                    for h in range(HEADS):
                        m = tr(ps[:, 4 + t % 2, h * DK:(h + 1) * DK], Tb[d][:, h, t * P:(t + 1) * P], ident)
                    m.then_inc(filled(f"ks{d}{t}"), 1)
            project("g0", "tm", w_in, COL_G, ada=(1, 2))
            project("g1", "tm", w_in, COL_G + NCOL, ada=(1, 2))

            def gla_updates(h):
                wait_read(pe, "act", "ks12")
                wait_read(pe, "act", "v1_2")
                for i in range(5):
                    for d in range(2):
                        c = SCAN[d][i][0]
                        r = CHUNK * (c % 2)
                        take(pe, 4 - d, f"upd{h}{i}{d}")
                        m = mm(ps[:, 4 - d, 0:DV], ksT[d][r:r + CHUNK, c // 2, h * DK:(h + 1) * DK],
                               vtm[r:r + CHUNK, c // 2, h * DV:(h + 1) * DV], start=True, stop=True)
                        m.then_inc(filled(f"upd{h}{i}{d}"), 1)

            def gla_scores(h, t):
                take(pe, 5, f"att{h}{t}")
                for d in range(2):
                    m = mm(ps[:, 5, d * P:(d + 1) * P], Bb[d][:, h, t * P:(t + 1) * P],
                           Pb[d][:, h, t * P:(t + 1) * P], start=True, stop=True)
                m.then_inc(filled(f"att{h}{t}"), 1)

            def gla_output(h, t):
                take(pe, t, f"o{h}{t}", ("act", "dve"))
                wait_read(pe, "dve", f"att{h}{t}")
                if t == 0:
                    wait_read(pe, "dve", f"upd{h}41")
                    pe.wait_ge(S("in_s0"), 32 * (h + 1))
                for d in range(2):
                    mm(ps[:, t, 0:DV], attm[:, t % 2, d, :], vtm[:, t, h * DV:(h + 1) * DV], start=(d == 0),
                       stop=False, skip_group_check=True)
                inter = [(d, c) for d in range(2) for c in (2 * t, 2 * t + 1) if c in STATE_IN[d]]
                for d, c in inter:
                    r = CHUNK * (c % 2)
                    m = mm(ps[r:r + CHUNK, t, 0:DV], Pb[d][:, h, c * CHUNK:(c + 1) * CHUNK],
                           Sst[:, d, STATE_IN[d][c], :], start=False, stop=(d, c) == inter[-1],
                           skip_group_check=True)
                m.then_inc(filled(f"o{h}{t}"), 1)

            def gla_head(h):
                gla_updates(h)
                gla_scores(h, 0)
                for t in range(NT):
                    if t + 1 < NT:
                        gla_scores(h, t + 1)
                    gla_output(h, t)

            def hy_turn(hb, part):
                wait_read(pe, "dve", f"hy{hb}{part}_3")
                for t in range(NT):
                    key = f"zx{hb}{part}{t}"
                    take(pe, 4 + t % 2, key, ("act",))
                    for m_ in range(4):
                        m = tr(ps[:, 4 + t % 2, m_ * P:(m_ + 1) * P], hyT[:, m_, t * P:(t + 1) * P], ident)
                    m.then_inc(filled(key), 1)

            def transform(src, rows, tiles, key, bank, readers):
                take(pe, bank, key, readers)
                for t in tiles:
                    m = mm(ps[:, bank, :], dft[:, FWD[t, rows], :], src(t), start=(t == tiles[0]),
                           stop=(t == tiles[-1]))
                m.then_inc(filled(key), 1)

            def filter_taps(ho):
                pe.wait_ge(S("in_w3"), 16 * (ho + 1))
                if ho == 0:
                    pe.wait_ge(S("hdn_ready"), 1)
                for t in range(NT):
                    for d in range(2):
                        take(pe, 4 + d, f"f{ho}{t}{d}")
                        mm(ps[:, 4 + d, :], hdn[:, t * P:(t + 1) * P], w3[:, d, :], start=True,
                           stop=True).then_inc(filled(f"f{ho}{t}{d}"), 1)

            def filter_norms(ho):
                pe.wait_ge(S("absf_ready"), NT * (ho + 1))
                for s, q in enumerate(SEQS):
                    take(pe, 4 + s, f"norm{ho}{s}")
                    for t in q["tiles"]:
                        m = mm(ps[:, 4 + s, :], ones[:, :], fs[:, t, :], start=(t == q["tiles"][0]),
                               stop=(t == q["tiles"][-1]))
                    m.then_inc(filled(f"norm{ho}{s}"), 1)

            def filter_spectrum(ho):
                if ho == 0:
                    pe.wait_ge(S("in_dft"), 16)
                pe.wait_ge(S("fsd_ready"), NT * (ho + 1))
                nth = 0
                for q in SEQS:
                    for r in q["re"]:
                        transform(lambda t: fs[:, t, :], r, q["tiles"], f"G{ho}{r}", 4 + nth % 2, ("act",))
                        nth += 1
                    for r in q["im"]:
                        transform(lambda t: ff[:, t, 0, :], r, q["tiles"], f"G{ho}{r}", 4 + nth % 2, ("act",))
                        nth += 1

            def long_conv(ho):
                wait_read(pe, "act", TURNED[ho])
                if ho % 2:
                    wait_read(pe, "dve", f"c{ho - 1}2")
                nth = 0
                for q in SEQS:
                    for re, im in zip(q["re"], q["im"]):
                        for r in (re, im):
                            transform(lambda t: zx[:, 0, t, :], r, q["tiles"], f"Z{ho}{r}", (4, 5, 0, 1, 2, 3)[nth],
                                      ("dve",))
                            nth += 1
                for _ in range((2, 2, 1, 0)[ho]):
                    ada_step()
                for s, q in enumerate(SEQS):
                    rows = q["re"] + q["im"]
                    pe.wait_ge(S("Y_ready"), 6 * ho + (2, 6)[s])
                    for t in q["tiles"]:
                        take(pe, t, f"c{ho}{t}")
                        for r in rows:
                            m = mm(ps[:, t, :], dft[:, INV[r, t], :], Yb[:, r, :], start=(r == rows[0]),
                                   stop=(r == rows[-1]))
                        m.then_inc(filled(f"c{ho}{t}"), 1)

            for (hb, part, ho), ada in zip(HYENA_BLOCKS, HYENA_ADA):
                if ho is not None:
                    filter_taps(ho)
                project(f"hy{hb}{part}", "fm", w_in, COL_HY + part * HYW + hb * HALF, readers=("act", "dve"),
                        ada=ada, between=None if ho is None else (lambda: filter_norms(ho)))
                if ho is None:
                    gla_head(2 * part)
                    gla_head(2 * part + 1)
                else:
                    filter_spectrum(ho)
                hy_turn(hb, part)
                if ho is not None:
                    long_conv(ho)
            assert ada_at[0] == 3 * KT

            for g in range(2):
                pe.wait_ge(*((S("ygla_ready"), NT * HEADS), (S("yhy_ready"), NT))[g])
                for kt in range(8):
                    take(pe, kt % 4, f"yT{g}{kt}", ("act",))
                    for t in range(NT):
                        src = gtm[:, t, kt * P:(kt + 1) * P] if g == 0 else \
                            z2[:, t, kt // 4, (kt % 4) * P:(kt % 4 + 1) * P]
                        m = tr(ps[:, kt % 4, t * P:(t + 1) * P], src, ident)
                    m.then_inc(filled(f"yT{g}{kt}"), 1)
            wait_read(pe, "act", "yT17")

            def gate_rows(ph, j):
                for c in range(2):
                    take(pe, 4 + c, f"gate{ph}{j}{c}")
                    mm(ps[:, 4 + c, :], sel[32 * j:32 * j + 2, c, :], mod[32 * j:32 * j + 2, 3 * ph + 2, :],
                       start=True, stop=True).then_inc(filled(f"gate{ph}{j}{c}"), 1)

            pe.wait_ge(S("mod_ready"), 4)
            for nb in range(4):
                gate_rows(0, nb)
                project(f"wo{nb}", "tm", w_out, nb * NCOL, readers=("act", "dve"),
                        banks=(0, 1, 2, 3) if nb % 2 == 0 else (3, 6, 7))
            modulate(1)

            wait_read(pe, "act", f"hT1_{KT - 1}")
            pe.wait_ge(S("in_router"), 64)
            take(pe, 2, "router")
            for t in range(NT):
                for k in range(KT):
                    m = mm(ps[:, 2, t * 32:t * 32 + NG + NE], hT[:, k, t * P:(t + 1) * P], wr[:, k, :],
                           start=(k == 0), stop=(k == KT - 1), skip_group_check=True)
            m.then_inc(filled("router"), 1)
            pe.wait_ge(S("pairs_ready"), 1)
            take(pe, 3, "rank")
            for t in range(NT):
                for s in range(t + 1):
                    mm(ps[:, 3, t * NE:(t + 1) * NE], tri if s == t else ones[:, :], r_pair[:, s, :], start=(s == 0),
                       stop=(s == t), skip_group_check=True)
            for s in range(NT):
                m = mm(ps[:, 3, NT * NE:(NT + 1) * NE], ones[:, :], r_pair[:, s, :], start=(s == 0),
                       stop=(s == NT - 1), skip_group_check=True)
            m.then_inc(filled("rank"), 1)

            def turn_rows():
                for i in range(2):
                    for q in range(8):
                        k = 8 * i + q
                        m = tr(ps[:, 2 + i, q * BLK:(q + 1) * BLK], hg[:, k * P:(k + 1) * P], ident[0:BLK, 0:BLK])
                    m.then_inc(S("x_turns"), 1)

            for j in range(4):
                gate_rows(1, j)
            for c in range(2):
                wait_read(pe, "dve", f"gate13{c}")
            pe.wait_ge(S("tables_ready"), 1)
            nblk = pe.value_load(tab_i[0:1, MAXB:MAXB + 1], min_val=NE, max_val=MAXB)
            for s in range(6):
                pe.sem_inc(S(f"used{s}"), 1)
            pe.sem_inc(S("x_turns"), 1)
            pe.wait_ge(S("x_gathered"), 16)
            turn_rows()
            with pe.Fori(0, nblk) as b:
                ex = pe.value_load(tab_i[0:1, bass.ds(b, 1)], min_val=0, max_val=NE - 1)
                pe.wait_ge(S("he_ready"), b + 1)
                pe.wait_ge(S("x_turned"), b * 2 + 2)
                for kh in range(2):
                    for which in range(2):
                        pe.wait_ge(S(f"w{2 * kh + which}"), ex * 16 + 16)
                    for k in range(8):
                        for which in range(2):
                            v = mring[2 * kh + which].rearrange("p (k n) -> p k n", k=8)
                            half = slice(BLK * which, BLK * (which + 1))
                            m = mm(ps[half, 0, :], hgT[:, kh * 8 + k, :], v[:, k, :], start=(kh + k == 0),
                                   stop=(kh * 8 + k == KT - 1), skip_group_check=True)
                            if k == 7:
                                m.then_inc(S(f"used{2 * kh + which}"), 1)
                pe.wait_ge(S("x_gathered"), b * 16 + 32)
                pe.nop(nofuse=True)
                turn_rows()
                pe.wait_ge(S("he_ready"), b + 2)
                pe.nop(nofuse=True)
                for q in range(4):
                    m = tr(ps[:, 1, q * BLK:(q + 1) * BLK], he[:, q * P:(q + 1) * P], ident[0:BLK, 0:BLK])
                m.then_inc(S("he_turns"), 1)
                pe.wait_ge(S("he_turned"), b + 2)
                pe.wait_ge(S("y_read_act"), b + 1)
                pe.wait_ge(S("y_read_dve"), b + 1)
                for kh in range(2):
                    pe.wait_ge(S(f"w{4 + kh}"), ex * 16 + 16)
                    v = mring[4 + kh].rearrange("p (k n) -> p k n", k=2)
                    for k in range(2):
                        for n in range(4):
                            half = slice(BLK * (n % 2), BLK * (n % 2 + 1))
                            m = mm(ps[half, 4 + n // 2, :], heT[:, 2 * kh + k, :], v[:, k, n * NCOL:(n + 1) * NCOL],
                                   start=(kh + k == 0), stop=(kh + k == 2), skip_group_check=True)
                    m.then_inc(S(f"used{4 + kh}"), 1)

        @block.sync
        def _(sp):
            sp.dma_start(rowsA[0:16, :], T["c_ctx"].rearrange("(k p) -> k p", p=P)).then_inc(S("in_rowsA"), 16)
            sp.dma_start(rowsA[16:32, :], T["c"][0].rearrange("(k p) -> k p", p=P)).then_inc(S("in_rowsA"), 16)
            sp.dma_start(rowsA[32:40, :], T["g_hy"][0].rearrange("(k p) -> k p", p=P)).then_inc(S("in_rowsA"), 16)
            sp.dma_start(rowsA[40:42, :], T["g_gla"][0].rearrange("(k p) -> k p", p=P)).then_inc(S("in_rowsA"), 16)
            sp.dma_start(rowsA[42:46, :], T["b_dec_f"][0].rearrange("(k p) -> k p", p=P)).then_inc(S("in_rowsA"), 16)
            sp.dma_start(rowsA[46:50, :], T["b_dec_b"][0].rearrange("(k p) -> k p", p=P)).then_inc(S("in_rowsA"), 16)
            sp.dma_start(base[:, :], T["k_base"]).then_inc(S("in_base"), 16)
            for i, src in enumerate(loads):
                if i >= RING:
                    sp.wait_ge(*released[i - RING])
                v = slot_view(i)
                if len(src.shape) == 3:
                    v = v.rearrange("p (k n) -> p k n", k=8)
                sp.dma_start(v, src).then_inc(S(f"ring{i % RING}"), 16)
            wu, wg, wd = T["w_exp_up"][0], T["w_exp_gate"][0], T["w_exp_down"][0]

            def expert_slot(s, ex):
                kt, part = (8, s // 2) if s < 4 else (2, s - 4)
                w = (wu, wg)[s % 2] if s < 4 else wd
                src = w[bass.ds(ex, 1), part * kt * P:(part + 1) * kt * P, :].rearrange("a (k p) n -> p (a k) n", p=P)
                sp.dma_start(mring[s].rearrange("p (k n) -> p k n", k=kt), src).then_inc(S(f"w{s}"), 16)

            for s in range(RING):
                sp.wait_ge(*released[max(i for i in range(len(loads)) if i % RING == s)])
                expert_slot(s, 0)
            wait_read(sp, "dve", "shift131")
            for t in range(NT):
                sp.dma_start(h_dram[t * P:(t + 1) * P, :], h_tm[:, t, :]).then_inc(S("h_stored"), 16)
            sp.wait_ge(S("h_stored"), 16 * NT)
            wait_read(sp, "act", f"hT1_{KT - 1}")
            for s in range(RING, 6):
                expert_slot(s, 0)
            sp.wait_ge(S("tables_ready"), 1)
            with sp.Fori(0, NE - 1) as e:
                done = sp.value_load(tab_i[0:1, bass.ds(e + (MAXB + 2), 1)], min_val=1, max_val=MAXB)
                for s in range(6):
                    sp.wait_ge(S(f"used{s}"), done + 1)
                    sp.nop(nofuse=True)
                    expert_slot(s, e + 1)
            for t in range(NT):
                sp.wait_ge(S("out_ready"), t + 1)
                sp.dma_start(out_rows[t], yga[t][0]).then_inc(S("out_done"), 16)
            sp.wait_ge(S("out_done"), 16 * NT)

        @block.gpsimd
        def _(pool):
            g = Engine(pool, S("pool_step"))
            g.op(nc.gpsimd.memset(sT[:, :, :], 0.0), S("sT_zero"))
            g.op(nc.gpsimd.memset(mod[:, :, :], 0.0), S("rows_zero"))
            g.op(nc.gpsimd.memset(gain[:, :, :], 0.0), S("rows_zero"))
            g.op(nc.gpsimd.memset(wdec, 0.0), S("wdec_zero"))
            g.op(nc.gpsimd.memset(ones[:, :], 1.0))
            g.op(nc.gpsimd.memset(attm[:, :, :, :], 0.0))
            g.op(nc.gpsimd.memset(reset[:, :], 1.0))
            g.op(nc.gpsimd.memset(zero_i, 0))
            g.op(nc.gpsimd.iota(tok_i[:, :], [[P, NT]], base=0, channel_multiplier=1))
            g.sync()
            g.op(nc.gpsimd.memset(reset[:, :].rearrange("p (c s) -> p c s", s=CHUNK)[:, :, 0:1], 0.0), S("pool_const"))
            pool.dma_start(tok_dram.rearrange("(a b) c -> a (b c)", b=P), zero_i).then_inc(S("tok_zero"), 16)

            for h in range(HEADS):
                if h == 0:
                    pool.wait_ge(S("ks_ready"), 2)
                else:
                    wait_read(pool, "dve", f"o{h - 1}2")
                pool.wait_ge(S("tok_zero"), 16)
                for d, name in enumerate(("state_gla_fwd", "state_gla_bwd")):
                    pool.dma_start(Sst[:, d, 2, :], T[name][0, 0, h]).then_inc(S("in_s0"), 16)
                wait_read(pool, "dve", f"upd{h}11")
                for d, name in enumerate(("new_fwd", "new_bwd")):
                    pool.dma_start(T[name][0, 0, h], Sst[:, d, 1, :]).then_inc(S("state_out"), 16)
            wait_read(pool, "dve", "o32")
            wait_read(pool, "act", "o32")
            pool.dma_start(dft, T["k_dft"].rearrange("p (i m) -> p i m", m=P)).then_inc(S("in_dft"), 16)
            w3v = T["hy_w3"][0].rearrange("h (d o c) -> h d o c", d=2, o=2)
            for hb in range(2):
                for o in range(2):
                    ho = 2 * hb + o
                    cols = slice(hb * HALF, (hb + 1) * HALF)
                    if ho > 0:
                        pool.wait_ge(S("fsd_ready"), NT * ho)
                    if o == 0:
                        pool.dma_start(decay, T["k_decay"][:, :, cols]).then_inc(S("in_decay"), 16)
                    pool.dma_start(w3, w3v[:, :, o, cols]).then_inc(S("in_w3"), 16)
                    pool.dma_start(biasr[0:1, :], T["hy_bias"][0, o:o + 1, cols]).then_inc(S("in_bias"), 16)
            wait_read(pool, "dve", "c32")
            wrg, wre = T["w_router_grp"][0], T["w_router_exp"][0]
            pool.dma_start(wr[:, :, 0:NG], wrg.rearrange("(k p) n -> p k n", p=P)).then_inc(S("in_router"), 16)
            pool.dma_start(wr[:, :, NG:NG + NE], wre.rearrange("(k p) n -> p k n", p=P)).then_inc(S("in_router"), 16)
            pool.dma_start(br[:, 0:NG], T["b_router_grp"].broadcast_to([P, NG])).then_inc(S("in_router"), 16)
            pool.dma_start(br[:, NG:NG + NE], T["b_router_exp"].broadcast_to([P, NE])).then_inc(S("in_router"), 16)
            for t in range(NT):
                pool.dma_start(x_sb[:, t, :], x_rows[t]).then_inc(S("in_x_again"), 16)

            pool.wait_ge(S("slots_ready"), 1)
            for r in range(2):
                for t in range(NT):
                    pool.indirect_dma_start(
                        out=tok_dram, out_offset=bass.IndirectOffsetOnAxis(ap=slot_i[:, r, t:t + 1], axis=0),
                        in_=tok_i[:, t:t + 1], in_offset=None).then_inc(S("tok_set"), 16)
            pool.wait_ge(S("tok_set"), 16 * 2 * NT)
            pool.wait_ge(S("h_stored"), 16 * NT)
            pool.wait_ge(S("tables_ready"), 1)
            nblk = pool.value_load(tab_i[0:1, MAXB:MAXB + 1], min_val=NE, max_val=MAXB)
            with pool.Fori(0, nblk + 1) as b:
                pool.wait_ge(S("x_turns"), b * 2 + 1)
                pool.nop(nofuse=True)
                pool.dma_start(idx_i[:, :], tok_dram[bass.ds(b * BLK, BLK), :]).then_inc(S("idx_in"), 16)
                pool.wait_ge(S("idx_in"), b * 16 + 16)
                pool.nop(nofuse=True)
                pool.indirect_dma_start(out=hg, out_offset=None, in_=h_dram,
                                        in_offset=bass.IndirectOffsetOnAxis(ap=idx_i[:, :], axis=0)
                                        ).then_inc(S("x_gathered"), 16)
            pool.wait_ge(S("y_stored"), nblk * 32 + 1)
            pool.nop(nofuse=True)
            nfree = pool.value_load(tab_i[0:1, MAXB + 1:MAXB + 2], min_val=1, max_val=MAXB + 1 - NE)
            pool.wait_ge(S("y_filled"), nfree * 16)
            pool.nop(nofuse=True)
            for t in range(NT):
                for r in range(2):
                    pool.indirect_dma_start(out=yga[t][r], out_offset=None, in_=y_dram,
                                            in_offset=bass.IndirectOffsetOnAxis(ap=slot_i[:, r, t:t + 1], axis=0)
                                            ).then_inc(S(f"y_gathered{t}{r}"), 16)

        @block.scalar
        def _(act):
            a = Engine(act, S("act_step"))
            A = nc.scalar.activation

            def load(dst, src, sem):
                act.dma_start(dst, src).then_inc(S(sem), 16)

            load(rowsB[0:72, :], T["hy_conv_w"][0].rearrange("j (m p) -> (j m) p", p=P), "in_rowsB")
            load(rowsB[72:96, :], T["hy_conv_b"][0].rearrange("(m p) -> m p", p=P), "in_rowsB")
            for dst, src in ((w1s, T["hy_w1"][0]), (w2s, T["hy_w2"][0]), (pe_sb, T["k_pe"]),
                             (fcol[:, 0:1], T["hy_b1"].rearrange("a h -> h a")),
                             (fcol[:, 1:2], T["hy_b2"].rearrange("a h -> h a")),
                             (fcol[:, 2:3], T["hy_freq"].rearrange("a h -> h a"))):
                load(dst, src, "in_mlp")
            for t in range(NT):
                load(x_sb[:, t, :], x_rows[t], "in_x")
            wait_read(act, "dve", "colA")
            act.wait_ge(S("sT_zero"), 1)
            for c in range(2):
                a.op(A(sT[:, :, c], colA[:, 16 * c:16 * c + 16], ACT.Silu), S("sT_ready"))
            act.wait_ge(S("rows_zero"), 2)
            bias = T["b_ada"][0].rearrange("(q j n) -> j q n", j=4, n=NCOL)
            for j in range(4):
                for c in range(2):
                    load(mod[32 * j + c:32 * j + c + 1, :, :], bias[j:j + 1], "in_rows")
            for i, name in enumerate(("g_pre_mix", "g_post_mix", "g_pre_ffn", "g_post_ffn")):
                src = T[name].rearrange("a (j n) -> (a j) n", j=4)
                for j in range(4):
                    for c in range(2):
                        load(gain[32 * j + c:32 * j + c + 1, i, :], src[j:j + 1], "in_rows")
            load(wlr, w_in[:, COL_LR:COL_LR + 2 * RANK].rearrange("(k p) n -> p k n", p=P), "in_lr")
            act.wait_ge(S("wdec_zero"), 1)
            load(wdec[0:RANK, 0, :], T["w_dec_f"][0], "in_dec")
            load(wdec[RANK:2 * RANK, 1, :], T["w_dec_b"][0], "in_dec")
            load(masks[:, :, :], T["k_masks"], "in_masks")

            act.wait_ge(S("sin_arg"), 1)
            a.op(A(ftmp[:, 1, :], ftmp[:, 0, :], ACT.Sin), S("hid_ready"))

            def squares(src, junk, col):
                a.sync()
                a.op(A(junk, src, ACT.Square, accum_out=stat[:, col:col + 1]))

            def roots(col, n, width):
                a.sync()
                s = stat[:, col:col + n]
                a.op(A(s, s, ACT.Sqrt, bias=stat[:, 62:63], scale=1.0 / width), S("rms"))

            act.wait_ge(S("in_x"), 16 * NT)
            for t in range(NT):
                squares(x_sb[:, t, :], h_tm[:, t, :], t)
            act.wait_ge(S("eps_ready"), 1)
            roots(0, NT, D)
            act.wait_ge(S("sin_arg"), 2)
            a.op(A(hdn[:, :], ftmp[:, 0, :], ACT.Sin), S("hdn_ready"))

            def h_columns(ph):
                for kt in range(KT):
                    key = f"hT{ph}_{kt}"
                    b = read(act, key)
                    a.op(A(hT[:, kt, :], ps[:, b, 0:TOK], ACT.Copy), freed("act", key))

            h_columns(0)
            b = read(act, "lr")
            a.op(A(lrT, ps[0:2 * RANK, b, 0:TOK], ACT.Copy), freed("act", "lr"))

            def copy_out(key, dst, func=ACT.Copy):
                b = read(act, key)
                n = dst.shape[-1]
                a.op(A(dst, ps[:, b, 0:n], func), freed("act", key))

            wait_read(act, "dve", "shift031")
            for m_ in range(4):
                copy_out(f"q_{m_}", qf[:, m_, :])
            for d in range(2):
                for h in range(HEADS):
                    b = read(act, f"la{d}{h}")
                    a.op(A(Tb[d][:, h, :], ps[:, b, 0:TOK], ACT.Abs, bias=colA[:, 42 + 4 * d + h:43 + 4 * d + h]),
                         freed("act", f"la{d}{h}"))
            for d in range(2):
                a.sync()
                a.op(A(Tb[d], Tb[d], ACT.Exp, scale=-1.0))
            for d in range(2):
                a.sync()
                a.op(A(Tb[d], Tb[d], ACT.Ln, bias=1.0), S("decay_log"))
            for m_ in range(4):
                copy_out(f"k_{m_}", kf[:, m_, :])
            for d in range(2):
                act.wait_ge(S("decay_sums"), d + 1)
                a.op(A(Pb[d], Bb[d], ACT.Exp, scale=1.0 / TAU), S("decay_exp"))
                a.op(A(Bb[d], Bb[d], ACT.Exp, scale=-1.0 / TAU), S("decay_exp"))
                a.op(A(Tb[d], Tb[d], ACT.Exp, scale=1.0 / TAU), S("decay_exp"))
            for i in range(2):
                for t in range(NT):
                    copy_out(f"v{i}_{t}", vtm[:, t, i * NCOL:(i + 1) * NCOL])
            for d in range(2):
                for t in range(NT):
                    copy_out(f"ks{d}{t}", ksT[d][:, t, :])
            for i in range(2):
                for t in range(NT):
                    copy_out(f"g{i}_{t}", gtm[:, t, i * NCOL:(i + 1) * NCOL], ACT.Silu)

            def head_squares(h):
                for t in range(NT):
                    b = read(act, f"o{h}{t}")
                    wait_read(act, "dve", f"o{h}{t}")
                    a.sync()
                    c = 8 + t * HEADS + h
                    a.op(A(junk, ps[:, b, 0:DV], ACT.Square, accum_out=stat[:, c:c + 1]), freed("act", f"o{h}{t}"))

            act.wait_ge(S("ks_ready"), 2)
            for hb, part, ho in HYENA_BLOCKS:
                if ho is not None:
                    for t in range(NT):
                        for d in range(2):
                            wait_read(act, "dve", f"f{ho}{t}{d}")
                            a.op(A((fs, Gs)[d][:, t, :], ff[:, t, d, :], ACT.Abs), S("abs_done"))
                for m_ in range(4):
                    key, c = f"hy{hb}{part}_{m_}", part * 8 + hb * 4 + m_
                    b = read(act, key)
                    a.op(A(hyT[:, m_, :], ps[:, b, 0:TOK], ACT.Identity, bias=colB[:, 72 + c:73 + c],
                           scale=colB[:, 24 + c:25 + c]), freed("act", key))
                if ho is None:
                    head_squares(2 * part)
                    head_squares(2 * part + 1)
                    if part == 1:
                        roots(8, NT * HEADS, DV)
                else:
                    for r in range(NROW):
                        copy_out(f"G{ho}{r}", Gs[:, r, :])
                if hb == 1:
                    wait_read(act, "dve", f"c{ho - 1}2")
                for t in range(NT):
                    copy_out(f"zx{hb}{part}{t}", zx[:, part, t, :])
            wait_read(act, "dve", "c32")
            for t in range(NT):
                squares(z2[:, t, :, :].rearrange("p a b -> p (a b)"), hyT.rearrange("p a b -> p (a b)")[:, 0:HYW], 20 + t)
            roots(20, NT, HYW)
            for g in range(2):
                for kt in range(8):
                    key = f"yT{g}{kt}"
                    b = read(act, key)
                    c = 40 + kt % 2 if g == 0 else 32 + kt
                    a.op(A(hT[:, 8 * g + kt, :], ps[:, b, 0:TOK], ACT.Copy, scale=colA[:, c:c + 1]), freed("act", key))
            for nb in range(4):
                for t in range(NT):
                    key = f"wo{nb}_{t}"
                    b = read(act, key)
                    wait_read(act, "dve", key)
                    if (nb, t) == (0, 0):
                        a.sync()
                    c = 36 + 4 * t + nb
                    a.op(A(h_tm[:, t, nb * NCOL:(nb + 1) * NCOL], ps[:, b, :], ACT.Square,
                           accum_out=stat[:, c:c + 1]), freed("act", key))
            act.wait_ge(S("squares_summed"), 1)
            roots(24, NT, D)
            for t in range(NT):
                act.wait_ge(S("x2_ready"), t + 1)
                squares(x_sb[:, t, :], h_tm[:, t, :], 28 + t)
            roots(28, NT, D)
            h_columns(1)
            act.wait_ge(S("exp_arg"), 1)
            a.op(A(r_ex.rearrange("p a t e -> p (a t e)"), r_ex.rearrange("p a t e -> p (a t e)"), ACT.Exp), S("exp_done"))

            def turned(value):
                for i in range(2):
                    act.wait_ge(S("x_turns"), value + i)
                    A(hgT[:, 8 * i:8 * i + 8, :].rearrange("p k s -> p (k s)"), ps[:, 2 + i, :],
                      ACT.Copy).then_inc(S("x_turned"), 1)

            act.wait_ge(S("tables_ready"), 1)
            nblk = act.value_load(tab_i[0:1, MAXB:MAXB + 1], min_val=NE, max_val=MAXB)
            nfree = act.value_load(tab_i[0:1, MAXB + 1:MAXB + 2], min_val=1, max_val=MAXB + 1 - NE)
            with act.Fori(0, nfree) as b:
                act.dma_start(y_dram[bass.ds(MAXB * BLK - b * BLK, BLK), :], x_sb[0:BLK, 0, :]).then_inc(S("y_filled"), 16)
            act.sem_inc(S("y_read_act"), 1)
            act.sem_inc(S("y_stored"), 1)
            turned(2)
            with act.Fori(0, nblk) as b:
                act.wait_ge(S("used3"), b + 2)
                act.wait_ge(S("he_ready"), b + 1)
                A(sg, ps[BLK:2 * BLK, 0, :], ACT.Silu).then_inc(S("sg_ready"), 1)
                turned(b * 2 + 4)
                act.wait_ge(S("used5"), b + 2)
                act.wait_ge(S("y_stored"), b * 32 + 1)
                A(ysl[:, 0, :], ps[:, 4, :], ACT.Copy).then_inc(S("y_read_act"), 1)
                act.wait_ge(S("y_read_act"), b + 2)
                act.wait_ge(S("y_read_dve"), b + 2)
                rows = y_dram[bass.ds(b * BLK, BLK), :].rearrange("r (a c n) -> r a c n", a=2, c=2)
                for c in range(2):
                    act.dma_start(rows[:, :, c, :], ysl[c * BLK:(c + 1) * BLK, :, :]).then_inc(S("y_stored"), 16)
            for t in range(NT):
                act.wait_ge(S("y_added"), t + 1)
                squares(yga[t][0], y_sb[:, 0, :], 32 + t)
                roots(32 + t, 1, D)
            act.wait_ge(S("state_out"), 16 * 2 * HEADS)

        @block.vector
        def _(dve):
            v = Engine(dve, S("dve_step"))
            ve = nc.vector
            rms_n = [0]

            def inverse_roots(col, n):
                rms_n[0] += 1
                dve.wait_ge(S("rms"), rms_n[0])
                v.op(ve.reciprocal(stat[:, col:col + n], stat[:, col:col + n]))
                v.sync()

            v.op(ve.memset(stat[:, 62:63], EPS), S("eps_ready"))
            b = read(dve, "colA")
            v.op(ve.tensor_copy(colA[:, :], ps[:, b, 0:50]), freed("dve", "colA"))
            b = read(dve, "colB")
            v.op(ve.tensor_copy(colB[:, :], ps[:, b, 0:96]), freed("dve", "colB"))

            def sine_argument(key, bcol):
                b = read(dve, key)
                u, n = ftmp[:, 0, :], ftmp[:, 1, :]
                v.op(ve.tensor_scalar(u, ps[0:HID, b, 0:TOK], fcol[:, bcol:bcol + 1], fcol[:, 2:3], ALU.add, ALU.mult),
                     freed("dve", key))
                v.sync()
                v.op(ve.tensor_scalar(n, u, 1 / (2 * math.pi), MAGIC, ALU.mult, ALU.add))
                v.sync()
                v.op(ve.tensor_scalar(n, n, MAGIC, None, ALU.subtract))
                v.sync()
                v.op(ve.scalar_tensor_tensor(out=u, in0=n, scalar=-TWO_PI_HI, in1=u, op0=ALU.mult, op1=ALU.add))
                v.sync()
                v.op(ve.scalar_tensor_tensor(out=u, in0=n, scalar=-TWO_PI_LO, in1=u, op0=ALU.mult, op1=ALU.add))
                v.sync()
                v.op(ve.tensor_scalar(u, u, PI_SAFE, -PI_SAFE, ALU.min, ALU.max), S("sin_arg"))

            dve.wait_ge(S("in_mlp"), 16 * 6)
            sine_argument("hid1", 0)

            def mod_row(q):
                b = read(dve, ADA_KEYS[q])
                dve.wait_ge(S("in_rows"), 16 * 40)
                v.op(ve.tensor_tensor(mod[:, q, :], mod[:, q, :], ps[:, b, :], ALU.add), freed("dve", ADA_KEYS[q]))
                if q % 3 == 0:
                    return
                v.sync()
                g = gain[:, {1: 0, 2: 1, 4: 2, 5: 3}[q], :]
                if q % 3 == 1:
                    v.op(ve.scalar_tensor_tensor(out=mod[:, q, :], in0=mod[:, q, :], scalar=1.0, in1=g, op0=ALU.add,
                                                 op1=ALU.mult), S("mod_ready"))
                else:
                    v.op(ve.tensor_tensor(mod[:, q, :], mod[:, q, :], g, ALU.mult), S("mod_ready"))

            mod_row(0)
            mod_row(1)
            sine_argument("hid2", 1)

            def modulate(ph, col):
                for j in range(4):
                    js = slice(j * NCOL, (j + 1) * NCOL)
                    for w in ("scale", "shift"):
                        for t in range(NT):
                            key = f"{w}{ph}{j}{COND[t]}"
                            b = read(dve, key)
                            sem = freed("dve", key) if t != 1 else None
                            if w == "scale":
                                v.op(ve.scalar_tensor_tensor(out=h_tm[:, t, js], in0=x_sb[:, t, js],
                                                             scalar=stat[:, col + t:col + t + 1], in1=ps[:, b, :],
                                                             op0=ALU.mult, op1=ALU.mult), sem)
                            else:
                                v.op(ve.tensor_tensor(h_tm[:, t, js], h_tm[:, t, js], ps[:, b, :], ALU.add), sem)
                        v.sync()

            inverse_roots(0, NT)
            modulate(0, 0)

            for d in range(2):
                for h in range(HEADS):
                    b = read(dve, f"la{d}{h}")
                    wait_read(dve, "act", f"la{d}{h}")
                    v.op(ve.tensor_scalar(Pb[d][:, h, :], ps[:, b, 0:TOK], colA[:, 42 + 4 * d + h:43 + 4 * d + h], 0.0,
                                          ALU.add, ALU.min), freed("dve", f"la{d}{h}"))
            dve.wait_ge(S("pool_const"), 1)
            LAST = (CHUNK - 1, 0)
            chunks = lambda x: x.rearrange("p h (c s) -> p (h c) s", s=CHUNK)
            for d in range(2):
                dve.wait_ge(S("decay_log"), d + 1)
                v.op(ve.tensor_tensor(Pb[d], Pb[d], Tb[d], ALU.subtract))
                v.sync()
                for h in range(HEADS):
                    s = slice(None, None, (1, -1)[d])
                    v.op(ve.tensor_tensor_scan(Bb[d][:, h, s], reset[:, :], Pb[d][:, h, s], 0.0, ALU.mult, ALU.add))
                v.sync()
                last = chunks(Bb[d])[:, :, LAST[d]:LAST[d] + 1].to_broadcast([P, HEADS * NCH, CHUNK])
                v.op(ve.tensor_tensor(chunks(Tb[d]), last, chunks(Bb[d]), ALU.subtract), S("decay_sums"))
            wait_read(dve, "act", "q_3")
            wait_read(dve, "act", "k_3")
            for d in range(2):
                dve.wait_ge(S("decay_exp"), 3 * (d + 1))
                v.op(ve.tensor_copy(decs[:, d, :, :].rearrange("p h c -> p (h c)"), chunks(Pb[d])[:, :, LAST[d]]))
                v.sync()
                v.op(ve.scalar_tensor_tensor(out=Pb[d], in0=qf, scalar=DK ** -0.5, in1=Pb[d], op0=ALU.mult,
                                             op1=ALU.mult))
                v.op(ve.tensor_tensor(Bb[d], kf, Bb[d], ALU.mult))
                v.op(ve.tensor_tensor(Tb[d], kf, Tb[d], ALU.mult), S("ks_ready"))
            mod_row(2)
            mod_row(3)

            def state_updates(h):
                for i in range(5):
                    if i == 1 and h > 0:
                        dve.wait_ge(S("state_out"), 32 * h)
                    if i == 2:
                        dve.wait_ge(S("in_s0"), 32 * (h + 1))
                    for d in range(2):
                        c, old, new = SCAN[d][i]
                        key = f"upd{h}{i}{d}"
                        upd, sem = ps[:, read(dve, key), 0:DV], freed("dve", key)
                        if old is None:
                            v.op(ve.tensor_copy(Sst[:, d, new, :], upd), sem)
                        else:
                            v.op(ve.scalar_tensor_tensor(out=Sst[:, d, new, :], in0=Sst[:, d, old, :],
                                                         scalar=decs[:, d, h, c:c + 1], in1=upd, op0=ALU.mult,
                                                         op1=ALU.add), sem)
                    v.sync()

            def mask_scores(h, t):
                b = read(dve, f"att{h}{t}")
                for d in range(2):
                    v.op(ve.copy_predicated(attm[:, t % 2, d, :], masks[:, d, :], ps[:, b, d * P:(d + 1) * P]),
                         freed("dve", f"att{h}{t}") if d == 1 else None)

            def gate_output(h, t):
                b = read(dve, f"o{h}{t}")
                o = gtm[:, t, h * DV:(h + 1) * DV]
                v.op(ve.tensor_tensor(o, ps[:, b, 0:DV], o, ALU.mult), freed("dve", f"o{h}{t}"))

            def gla_head(h):
                state_updates(h)
                mask_scores(h, 0)
                for t in range(NT):
                    if t + 1 < NT:
                        mask_scores(h, t + 1)
                    gate_output(h, t)

            dve.wait_ge(S("in_masks"), 16)
            dve.wait_ge(S("tok_zero"), 16)
            wait_read(dve, "act", "g1_2")

            def short_conv(hb, part):
                for m_ in range(4):
                    key, c = f"hy{hb}{part}_{m_}", part * 8 + hb * 4 + m_
                    b = read(dve, key)
                    wait_read(dve, "act", key)
                    u, y = ps[:, b, 0:TOK], hyT[:, m_, :]
                    uw = u[:, SEQ:TOK].rearrange("p (r s) -> p r s", s=CHUNK)
                    yw = y[:, SEQ:TOK].rearrange("p (r s) -> p r s", s=CHUNK)
                    for tap, w in ((0, colB[:, c:c + 1]), (2, colB[:, 48 + c:49 + c])):
                        to = lambda n: slice(1, n) if tap == 0 else slice(0, n - 1)
                        fr = lambda n: slice(0, n - 1) if tap == 0 else slice(1, n)
                        v.op(ve.scalar_tensor_tensor(out=y[:, to(SEQ)], in0=u[:, fr(SEQ)], scalar=w, in1=y[:, to(SEQ)],
                                                     op0=ALU.mult, op1=ALU.add))
                        v.op(ve.scalar_tensor_tensor(out=yw[:, :, to(CHUNK)], in0=uw[:, :, fr(CHUNK)], scalar=w,
                                                     in1=yw[:, :, to(CHUNK)], op0=ALU.mult, op1=ALU.add),
                             freed("dve", key) if tap == 2 else None)
                        if tap == 0:
                            v.sync()

            def filters(ho):
                dve.wait_ge(S("in_decay"), 16 * (ho // 2 + 1))
                for t in range(NT):
                    for d in range(2):
                        b = read(dve, f"f{ho}{t}{d}")
                        v.op(ve.tensor_tensor(ff[:, t, d, :], ps[:, b, :], decay[:, t, :], ALU.mult),
                             freed("dve", f"f{ho}{t}{d}"))
                for t in range(NT):
                    dve.wait_ge(S("abs_done"), 2 * (NT * ho + t + 1))
                    v.op(ve.tensor_tensor(fs[:, t, :], fs[:, t, :], Gs[:, t, :], ALU.add), S("absf_ready"))
                for s in range(2):
                    b = read(dve, f"norm{ho}{s}")
                    v.op(ve.reciprocal(Gs[:, 3 + s, :], ps[:, b, :]), freed("dve", f"norm{ho}{s}"))
                for q in SEQS:
                    v.op(ve.memset(ff[0:1, q["tiles"][0], 1, :], 0.0))
                dve.wait_ge(S("in_bias"), 16 * (ho + 1))
                v.sync()
                for s, q in enumerate(SEQS):
                    for t in q["tiles"]:
                        for d in range(2):
                            v.op(ve.tensor_tensor(ff[:, t, d, :], ff[:, t, d, :], Gs[:, 3 + s, :], ALU.mult))
                v.sync()
                for q in SEQS:
                    f0 = ff[0:1, q["tiles"][0], 0, :]
                    v.op(ve.tensor_tensor(f0, f0, biasr[0:1, :], ALU.add))
                v.sync()
                for t in range(NT):
                    v.op(ve.tensor_tensor(fs[:, t, :], ff[:, t, 0, :], ff[:, t, 1, :], ALU.add))
                    v.op(ve.tensor_tensor(ff[:, t, 0, :], ff[:, t, 0, :], ff[:, t, 1, :], ALU.subtract), S("fsd_ready"))

            def long_conv(ho):
                wait_read(dve, "act", f"G{ho}5")
                for q in SEQS:
                    for re, im in zip(q["re"], q["im"]):
                        zr, zi = read(dve, f"Z{ho}{re}"), read(dve, f"Z{ho}{im}")
                        v.op(ve.tensor_tensor(Yb[:, re, :], ps[:, zr, :], Gs[:, re, :], ALU.mult))
                        v.op(ve.tensor_tensor(tA, ps[:, zi, :], Gs[:, im, :], ALU.mult))
                        v.op(ve.tensor_tensor(Yb[:, im, :], ps[:, zr, :], Gs[:, im, :], ALU.mult), freed("dve", f"Z{ho}{re}"))
                        v.op(ve.tensor_tensor(tB, ps[:, zi, :], Gs[:, re, :], ALU.mult), freed("dve", f"Z{ho}{im}"))
                        v.sync()
                        v.op(ve.tensor_tensor(Yb[:, re, :], Yb[:, re, :], tA, ALU.subtract), S("Y_ready"))
                        v.op(ve.tensor_tensor(Yb[:, im, :], Yb[:, im, :], tB, ALU.add), S("Y_ready"))
                        v.sync()
                wait_read(dve, "act", TURNED[ho])
                if ho == 1:
                    dve.wait_ge(S("state_out"), 32 * HEADS)
                for t in range(NT):
                    b = read(dve, f"c{ho}{t}")
                    dst = zx[:, 0, t, :] if ho % 2 == 0 else z2[:, t, ho // 2, :]
                    v.op(ve.tensor_tensor(dst, ps[:, b, :], zx[:, 1 + ho % 2, t, :], ALU.mult), freed("dve", f"c{ho}{t}"))

            for hb, part, ho in HYENA_BLOCKS:
                if ho is not None:
                    filters(ho)
                short_conv(hb, part)
                if ho is None:
                    gla_head(2 * part)
                    gla_head(2 * part + 1)
                    if part == 1:
                        inverse_roots(8, NT * HEADS)
                        for t in range(NT):
                            for h in range(HEADS):
                                o, c = gtm[:, t, h * DV:(h + 1) * DV], 8 + t * HEADS + h
                                v.op(ve.tensor_scalar(o, o, stat[:, c:c + 1], None, ALU.mult), S("ygla_ready"))
                else:
                    long_conv(ho)
                if ho == 2:
                    mod_row(4)
                    mod_row(5)
            inverse_roots(20, NT)
            for t in range(NT):
                z = z2[:, t, :, :].rearrange("p a b -> p (a b)")
                v.op(ve.tensor_scalar(z, z, stat[:, 20 + t:21 + t], None, ALU.mult), S("yhy_ready"))

            for nb in range(4):
                js = slice(nb * NCOL, (nb + 1) * NCOL)
                for t in range(NT):
                    key = f"gate0{nb}{COND[t]}"
                    b = read(dve, key)
                    v.op(ve.tensor_copy(y_sb[:, t, js], ps[:, b, :]), freed("dve", key) if t != 1 else None)
                v.sync()
                for t in range(NT):
                    b = read(dve, f"wo{nb}_{t}")
                    v.op(ve.tensor_tensor(y_sb[:, t, js], y_sb[:, t, js], ps[:, b, :], ALU.mult), freed("dve", f"wo{nb}_{t}"))
            wait_read(dve, "act", "wo3_2")
            v.op(ve.tensor_reduce(stat[:, 24:24 + NT], stat[:, 36:36 + 4 * NT].rearrange("p (t n) -> p t n", n=4), AX.X,
                                  ALU.add), S("squares_summed"))
            inverse_roots(24, NT)
            dve.wait_ge(S("in_x_again"), 16 * NT)
            for t in range(NT):
                v.op(ve.scalar_tensor_tensor(out=x_sb[:, t, :], in0=y_sb[:, t, :], scalar=stat[:, 24 + t:25 + t],
                                             in1=x_sb[:, t, :], op0=ALU.mult, op1=ALU.add), S("x2_ready"))
            inverse_roots(28, NT)
            modulate(1, 28)

            b = read(dve, "router")
            lg = ps[:, b, 0:NT * 32].rearrange("p (t e) -> p t e", e=32)[:, :, 0:NG + NE]
            dve.wait_ge(S("in_router"), 64)

            def step(ins, sem=None):
                v.op(ins, sem)
                v.sync()

            def over(x, n):
                return x.unsqueeze(2).to_broadcast([P, NT, n])

            step(ve.tensor_tensor(r_log, lg, br.unsqueeze(1).to_broadcast([P, NT, NG + NE]), ALU.add), freed("dve", "router"))
            for i in range(4):
                v.op(ve.memset(r_pri[:, :, i:i + 1], float(4 - i)))
            v.sync()

            def first_largest(x, out, top):
                step(ve.tensor_reduce(top, x, AX.X, ALU.max))
                step(ve.tensor_tensor(r_t4, x, over(top, 4), ALU.is_equal))
                step(ve.tensor_tensor(r_t4, r_t4, r_pri, ALU.mult))
                step(ve.tensor_reduce(r_t1, r_t4, AX.X, ALU.max))
                step(ve.tensor_tensor(out, r_t4, over(r_t1, 4), ALU.is_equal))

            glog, elog = r_log[:, :, 0:NG], r_log[:, :, NG:NG + NE]
            first_largest(glog, r_grp, r_top)
            step(ve.tensor_tensor(r_ex[:, 0], glog, over(r_top, 4), ALU.subtract))
            for g in range(NG):
                e4 = elog[:, :, g * EPG:(g + 1) * EPG]
                gg = r_grp[:, :, g:g + 1].to_broadcast([P, NT, EPG])
                step(ve.tensor_tensor(r_t4 if g else r_ex[:, 1], e4, gg, ALU.mult))
                if g:
                    step(ve.tensor_tensor(r_ex[:, 1], r_ex[:, 1], r_t4, ALU.add))
            step(ve.tensor_reduce(r_top, r_ex[:, 1], AX.X, ALU.max))
            step(ve.tensor_tensor(r_ex[:, 1], r_ex[:, 1], over(r_top, 4), ALU.subtract), S("exp_arg"))
            dve.wait_ge(S("exp_done"), 1)
            step(ve.tensor_reduce(r_pg, r_ex[:, 0], AX.X, ALU.add))
            step(ve.reciprocal(r_pg, r_pg))
            first_largest(r_ex[:, 1], r_oh[:, 0], r_top)
            step(ve.scalar_tensor_tensor(out=r_ex[:, 0], in0=r_oh[:, 0], scalar=-2.0, in1=r_ex[:, 1], op0=ALU.mult,
                                         op1=ALU.add))
            first_largest(r_ex[:, 0], r_oh[:, 1], r_m2)
            step(ve.tensor_tensor(r_t1, r_m2, r_top, ALU.add))
            step(ve.reciprocal(r_t1, r_t1))
            step(ve.tensor_tensor(r_pg, r_pg, r_t1, ALU.mult))
            step(ve.tensor_tensor(wpair[:, 0, :], r_pg, r_top, ALU.mult))
            step(ve.tensor_tensor(wpair[:, 1, :], r_pg, r_m2, ALU.mult))
            for r in range(2):
                for g in range(NG):
                    gg = r_grp[:, :, g:g + 1].to_broadcast([P, NT, EPG])
                    v.op(ve.tensor_tensor(r_one[:, r, :, g * EPG:(g + 1) * EPG], r_oh[:, r], gg, ALU.mult))
            v.sync()
            step(ve.tensor_tensor(r_pair, r_one[:, 0], r_one[:, 1], ALU.add), S("pairs_ready"))
            b = read(dve, "rank")
            count = ps[:, b, NT * NE:(NT + 1) * NE]
            step(ve.tensor_scalar(r_nb, count, BLK + 0.5, 1.0, ALU.is_gt, ALU.add))
            for n in range(2, TOK // BLK):
                step(ve.scalar_tensor_tensor(out=r_nb, in0=count, scalar=n * BLK + 0.5, in1=r_nb, op0=ALU.is_gt,
                                             op1=ALU.add))
            step(ve.tensor_tensor_scan(r_end, ones[:, 0:NE], r_nb, 0.0, ALU.mult, ALU.add))
            step(ve.tensor_tensor(r_first, r_end, r_nb, ALU.subtract))
            step(ve.tensor_scalar(r_first, r_first, float(BLK), None, ALU.mult))
            rank = ps[:, b, 0:NT * NE].rearrange("p (t e) -> p t e", e=NE)
            step(ve.tensor_tensor(r_slot, rank, r_first.unsqueeze(1).to_broadcast([P, NT, NE]), ALU.add),
                 freed("dve", "rank"))
            for r in range(2):
                step(ve.tensor_tensor(r_one[:, r], r_one[:, r], r_slot, ALU.mult))
                step(ve.tensor_reduce(r_t1, r_one[:, r], AX.X, ALU.add))
                step(ve.tensor_copy(slot_i[:, r, :], r_t1), S("slots_ready") if r else None)
            for n in range(MAXB):
                v.op(ve.tensor_scalar(r_cmp[:, n, :], r_end, float(n), None, ALU.is_le, ALU.add, accum_out=r_tab[:, n:n + 1]))
            step(ve.tensor_copy(r_tab[:, MAXB:MAXB + 1], r_end[:, NE - 1:NE]))
            v.op(ve.tensor_copy(r_tab[:, MAXB + 2:MAXB + 2 + NE], r_end))
            v.op(ve.tensor_scalar(r_tab[:, MAXB + 1:MAXB + 2], r_end[:, NE - 1:NE], -1.0, float(MAXB + 1), ALU.mult,
                                  ALU.add))
            step(ve.tensor_scalar(r_tab[:, 0:MAXB], r_tab[:, 0:MAXB], float(NE - 1), None, ALU.min))
            v.op(ve.tensor_copy(tab_i[:, :], r_tab), S("tables_ready"))

            dve.wait_ge(S("tables_ready"), 1)
            for j in range(4):
                for c in range(2):
                    b = read(dve, f"gate1{j}{c}")
                    v.op(ve.tensor_copy(gate_b[:, c, j * NCOL:(j + 1) * NCOL], ps[:, b, :]), freed("dve", f"gate1{j}{c}"))

            nblk = dve.value_load(tab_i[0:1, MAXB:MAXB + 1], min_val=NE, max_val=MAXB)
            for name in ("he_ready", "he_turned", "y_read_dve"):
                dve.sem_inc(S(name), 1)
            with dve.Fori(0, nblk) as b:
                dve.wait_ge(S("used3"), b + 2)
                dve.wait_ge(S("sg_ready"), b + 1)
                ve.tensor_tensor(he, sg, ps[0:BLK, 0, :], ALU.mult).then_inc(S("he_ready"), 1)
                dve.wait_ge(S("he_turns"), b + 1)
                ve.tensor_copy(heT.rearrange("p k s -> p (k s)"), ps[:, 1, 0:4 * BLK]).then_inc(S("he_turned"), 1)
                dve.wait_ge(S("used5"), b + 2)
                dve.wait_ge(S("y_stored"), b * 32 + 1)
                ve.tensor_copy(ysl[:, 1, :], ps[:, 5, :]).then_inc(S("y_read_dve"), 1)
            dve.wait_ge(S("y_stored"), nblk * 32 + 1)
            dve.nop(nofuse=True)

            def combine(t):
                dve.wait_ge(S(f"y_gathered{t}0"), 16)
                y0, y1 = yga[t]
                v.op(ve.tensor_scalar(y0, y0, wpair[:, 0, t:t + 1], None, ALU.mult))
                v.sync()
                dve.wait_ge(S(f"y_gathered{t}1"), 16)
                v.op(ve.scalar_tensor_tensor(out=y0, in0=y1, scalar=wpair[:, 1, t:t + 1], in1=y0, op0=ALU.mult,
                                             op1=ALU.add), S("y_added"))
                v.sync()
                v.op(ve.tensor_tensor(y1, y0, gate_b[:, COND[t], :], ALU.mult))

            def add_residual(t):
                inverse_roots(32 + t, 1)
                v.op(ve.scalar_tensor_tensor(out=yga[t][0], in0=yga[t][1], scalar=stat[:, 32 + t:33 + t],
                                             in1=x_sb[:, t, :], op0=ALU.mult, op1=ALU.add), S("out_ready"))

            combine(0)
            for t in range(1, NT):
                combine(t)
                add_residual(t - 1)
            add_residual(NT - 1)


_INS = ["x_prompt", "x_sample", "c", "state_gla_fwd", "state_gla_bwd", "c_ctx", "w_ada", "b_ada", "g_pre_mix",
        "g_post_mix", "g_pre_ffn", "g_post_ffn", "w_in", "w_dec_f", "b_dec_f", "w_dec_b", "b_dec_b", "g_gla",
        "hy_conv_w", "hy_conv_b", "hy_w1", "hy_b1", "hy_w2", "hy_b2", "hy_w3", "hy_freq", "hy_bias", "g_hy", "w_out",
        "w_router_grp", "b_router_grp", "w_router_exp", "b_router_exp", "w_exp_gate", "w_exp_up", "w_exp_down"]
_OUTS = [("y_prompt", (1, SEQ, D)), ("y_sample", (1, DEC, D)), ("new_fwd", (1, 1, HEADS, DK, DV)),
         ("new_bwd", (1, 1, HEADS, DK, DV))]


def kernel(**inputs):
    import concourse.bacc as bacc
    from concourse.bass_utils import run_bass_kernel_spmd

    nc = bacc.Bacc("TRN2", target_bir_lowering=False, num_devices=1)
    arrays = {name: np.ascontiguousarray(inputs[name]) for name in _INS}
    arrays.update(shape_constants())
    T = {name: nc.dram_tensor("in_" + name, a.shape, mybir.dt.from_np(a.dtype), kind="ExternalInput").ap()
         for name, a in arrays.items()}
    for name, shape in _OUTS:
        T[name] = nc.dram_tensor("out_" + name, shape, F32, kind="ExternalOutput").ap()
    build(nc, T)
    r = run_bass_kernel_spmd(nc, [{"in_" + name: a for name, a in arrays.items()}], core_ids=[0])
    return tuple(r.results[0]["out_" + name] for name, _ in _OUTS)
```
